# Optimizing a Trainium2 kernel written in Bass

```python
import math
import jax, jax.numpy as jnp
from jax import lax
import numpy as np

D_MODEL = 2048
BATCH = 1
SEQ = 256
DEPTH = 1
DEC_BATCH = 8
DEC_SEQ = 4
PAST_LEN = 1024
PAGE_SIZE = 128

ATTN_WIDTH = D_MODEL // 2
SSM_WIDTH = D_MODEL - ATTN_WIDTH
HEAD_DIM = 64
N_HEADS = ATTN_WIDTH // HEAD_DIM
N_KV_HEADS = 4
Q_PER_KV = N_HEADS // N_KV_HEADS
KV_WIDTH = N_KV_HEADS * HEAD_DIM
WINDOW = 128
BLOCK = 128
SSM_GROUP = 16
N_SSM_GROUPS = SSM_WIDTH // SSM_GROUP
STATE_DIM = 64
D_FF = 4 * D_MODEL
PROJ_WIDTH = ATTN_WIDTH + 2 * KV_WIDTH + SSM_WIDTH
EPS = 1e-6
NEG_INF = -1e30
DT_MIN = 1e-3
DT_MAX = 1e-1

kernel_name = 'hymba_swa_sink_s5_step'

def rmsnorm(x, g):
    xf = x.astype(jnp.float32)
    r = lax.rsqrt(jnp.mean(xf * xf, axis=-1, keepdims=True) + EPS)
    return (xf * r * g.astype(jnp.float32)).astype(x.dtype)

def alibi_slopes():
    h = jnp.arange(1, N_HEADS + 1, dtype=jnp.float32)
    return jnp.exp2(-8.0 * h / N_HEADS).reshape(N_KV_HEADS, Q_PER_KV)

def split_projection(z):
    n, t = z.shape[:2]
    o1 = ATTN_WIDTH
    o2 = o1 + KV_WIDTH
    o3 = o2 + KV_WIDTH
    q = z[..., :o1].reshape(n, t, N_KV_HEADS, Q_PER_KV, HEAD_DIM)
    k = z[..., o1:o2].reshape(n, t, N_KV_HEADS, HEAD_DIM)
    v = z[..., o2:o3].reshape(n, t, N_KV_HEADS, HEAD_DIM)
    u = z[..., o3:]
    return q, k, v, u

def band_probs(scores, delta, valid, slopes, sinks):
    s = scores - slopes[:, :, None, None] * delta.astype(jnp.float32)
    s = jnp.where(valid, s, NEG_INF)
    sink = sinks[:, :, None]
    m = jnp.maximum(jnp.max(s, axis=-1), sink)
    p = jnp.exp(s - m[..., None])
    denom = jnp.sum(p, axis=-1) + jnp.exp(sink - m)
    return p / denom[..., None]

def prompt_window_attention(q, k, v, slopes, sinks):
    b, s = q.shape[:2]
    nb = s // BLOCK
    qb = q.reshape(b, nb, BLOCK, N_KV_HEADS, Q_PER_KV, HEAD_DIM)
    pad = jnp.zeros((b, BLOCK, N_KV_HEADS, HEAD_DIM), k.dtype)
    kp = jnp.concatenate([pad, k], axis=1).reshape(b, nb + 1, BLOCK, N_KV_HEADS, HEAD_DIM)
    vp = jnp.concatenate([pad, v], axis=1).reshape(b, nb + 1, BLOCK, N_KV_HEADS, HEAD_DIM)
    kb = jnp.concatenate([kp[:, :-1], kp[:, 1:]], axis=2)
    vb = jnp.concatenate([vp[:, :-1], vp[:, 1:]], axis=2)
    scores = jnp.einsum('bnqkrd,bnskd->bnkrqs', qb, kb,
                        preferred_element_type=jnp.float32) * (HEAD_DIM ** -0.5)
    i = jnp.arange(BLOCK)[:, None]
    j = jnp.arange(2 * BLOCK)[None, :]
    delta = i + BLOCK - j
    key_pos = jnp.arange(nb)[:, None, None] * BLOCK - BLOCK + j[None]
    valid = (delta >= 0) & (delta <= WINDOW) & (key_pos >= 0)
    p = band_probs(scores, delta, valid[:, None, None], slopes, sinks)
    out = jnp.einsum('bnkrqs,bnskd->bnqkrd', p.astype(v.dtype), vb)
    return out.reshape(b, s, ATTN_WIDTH)

def sample_window_attention(q, k_new, v_new, cache_k, cache_v, slopes, sinks):
    n, t = q.shape[:2]
    k_all = jnp.concatenate([cache_k.astype(k_new.dtype), k_new], axis=1)
    v_all = jnp.concatenate([cache_v.astype(v_new.dtype), v_new], axis=1)
    scores = jnp.einsum('nqkrd,nskd->nkrqs', q, k_all,
                        preferred_element_type=jnp.float32) * (HEAD_DIM ** -0.5)
    i = jnp.arange(t)[:, None]
    j = jnp.arange(WINDOW + t)[None, :]
    delta = i + WINDOW - j
    valid = (delta >= 0) & (delta <= WINDOW)
    p = band_probs(scores, delta, valid, slopes, sinks)
    out = jnp.einsum('nkrqs,nskd->nqkrd', p.astype(v_all.dtype), v_all)
    return out.reshape(n, t, ATTN_WIDTH), k_all[:, -WINDOW:], v_all[:, -WINDOW:]

def ssm_discretize(A_re, A_im, log_dt, B_re, B_im):
    A = lax.complex(A_re.astype(jnp.float32), A_im.astype(jnp.float32))
    dt = jnp.exp(log_dt.astype(jnp.float32))[:, None]
    A_bar = jnp.exp(A * dt)
    B = lax.complex(B_re.astype(jnp.float32), B_im.astype(jnp.float32))
    B_bar = ((A_bar - 1.0) / A)[..., None] * B
    return A_bar, B_bar

def ssm_combine(e1, e2):
    a1, b1 = e1
    a2, b2 = e2
    return a1 * a2, a2 * b1 + b2

def ssm_mixer(u, h0_re, h0_im, A_bar, B_bar, C_re, C_im, D_skip):
    n, t = u.shape[:2]
    uf = u.astype(jnp.float32).reshape(n, t, N_SSM_GROUPS, SSM_GROUP)
    bu = jnp.einsum('ntgh,gph->ntgp', uf.astype(jnp.complex64), B_bar)
    h0 = lax.complex(h0_re.astype(jnp.float32), h0_im.astype(jnp.float32))
    bu = bu.at[:, 0].add(A_bar * h0)
    a = jnp.broadcast_to(A_bar, bu.shape)
    _, h = lax.associative_scan(ssm_combine, (a, bu), axis=1)
    C = lax.complex(C_re.astype(jnp.float32), C_im.astype(jnp.float32))
    y = jnp.real(jnp.einsum('ntgp,ghp->ntgh', h, C)) \
        + D_skip.astype(jnp.float32).reshape(N_SSM_GROUPS, SSM_GROUP) * uf
    h_last = h[:, -1]
    return y.reshape(n, t, SSM_WIDTH), jnp.real(h_last), jnp.imag(h_last)

def hybrid_layer(x, cache_k, cache_v, h0_re, h0_im, p):
    t = x.shape[1]
    z = rmsnorm(x, p['attn_norm_g']) @ p['w_in']
    q, k, v, u = split_projection(z)
    q = rmsnorm(q, p['q_norm_g'])
    k = rmsnorm(k, p['k_norm_g'])
    slopes = alibi_slopes()
    sinks = p['attn_sinks'].astype(jnp.float32).reshape(N_KV_HEADS, Q_PER_KV)
    if cache_k is None:
        attn = prompt_window_attention(q, k, v, slopes, sinks)
        new_k = k[:, t - WINDOW:]
        new_v = v[:, t - WINDOW:]
    else:
        attn, new_k, new_v = sample_window_attention(q, k, v, cache_k, cache_v, slopes, sinks)
    A_bar, B_bar = ssm_discretize(p['ssm_A_re'], p['ssm_A_im'], p['ssm_log_dt'],
                                  p['ssm_B_re'], p['ssm_B_im'])
    y_ssm, h_re, h_im = ssm_mixer(u, h0_re, h0_im, A_bar, B_bar,
                                  p['ssm_C_re'], p['ssm_C_im'], p['ssm_D'])
    g = jax.nn.gelu(y_ssm)
    ssm_out = (g * jax.nn.sigmoid(g @ p['w_glu'].astype(jnp.float32)
                                  + p['b_glu'].astype(jnp.float32))).astype(x.dtype)
    mix = jnp.concatenate([rmsnorm(attn, p['attn_out_g']),
                           rmsnorm(ssm_out, p['ssm_out_g'])], axis=-1)
    h = x + mix @ p['w_out']
    y = h + jnp.square(jax.nn.relu(rmsnorm(h, p['mlp_norm_g']) @ p['w_mlp_up'])) @ p['w_mlp_down']
    return y, new_k, new_v, h_re.astype(h0_re.dtype), h_im.astype(h0_im.dtype)

def setup_inputs(seed: int = 0) -> dict:
    key = jax.random.key(seed)
    ks = jax.random.split(key, 32)
    f32 = jnp.float32
    nrm = lambda k, shape, s: jax.random.normal(k, shape, f32) * s
    gain = lambda k, shape: 1.0 + 0.05 * jax.random.normal(k, shape, f32)
    L = DEPTH
    G, P, H = N_SSM_GROUPS, STATE_DIM, SSM_GROUP
    a_im_base = math.pi * jnp.arange(P, dtype=f32)
    return {
        'x_prompt': nrm(ks[0], (BATCH, SEQ, D_MODEL), 1.0),
        'x_sample': nrm(ks[1], (DEC_BATCH, DEC_SEQ, D_MODEL), 1.0),
        'cache_k': nrm(ks[2], (L, DEC_BATCH, WINDOW, N_KV_HEADS, HEAD_DIM), 1.0),
        'cache_v': nrm(ks[3], (L, DEC_BATCH, WINDOW, N_KV_HEADS, HEAD_DIM), 1.0),
        'state_ssm_re': nrm(ks[4], (L, DEC_BATCH, G, P), 0.3),
        'state_ssm_im': nrm(ks[5], (L, DEC_BATCH, G, P), 0.3),
        'attn_norm_g': gain(ks[6], (L, D_MODEL)),
        'w_in': nrm(ks[7], (L, D_MODEL, PROJ_WIDTH), D_MODEL ** -0.5),
        'q_norm_g': gain(ks[8], (L, HEAD_DIM)),
        'k_norm_g': gain(ks[9], (L, HEAD_DIM)),
        'attn_sinks': nrm(ks[10], (L, N_HEADS), 1.0),
        'ssm_A_re': -0.5 + 0.01 * jax.random.normal(ks[11], (L, G, P), f32),
        'ssm_A_im': a_im_base + 0.01 * jax.random.normal(ks[12], (L, G, P), f32),
        'ssm_log_dt': jax.random.uniform(ks[13], (L, G), f32, math.log(DT_MIN), math.log(DT_MAX)),
        'ssm_B_re': nrm(ks[14], (L, G, P, H), (2 * H) ** -0.5),
        'ssm_B_im': nrm(ks[15], (L, G, P, H), (2 * H) ** -0.5),
        'ssm_C_re': nrm(ks[16], (L, G, H, P), (2 * P) ** -0.5),
        'ssm_C_im': nrm(ks[17], (L, G, H, P), (2 * P) ** -0.5),
        'ssm_D': nrm(ks[18], (L, SSM_WIDTH), 1.0),
        'w_glu': nrm(ks[19], (L, SSM_WIDTH, SSM_WIDTH), SSM_WIDTH ** -0.5),
        'b_glu': nrm(ks[20], (L, SSM_WIDTH), 0.01),
        'attn_out_g': gain(ks[21], (L, ATTN_WIDTH)),
        'ssm_out_g': gain(ks[22], (L, SSM_WIDTH)),
        'w_out': nrm(ks[23], (L, D_MODEL, D_MODEL), D_MODEL ** -0.5),
        'mlp_norm_g': gain(ks[24], (L, D_MODEL)),
        'w_mlp_up': nrm(ks[25], (L, D_MODEL, D_FF), D_MODEL ** -0.5),
        'w_mlp_down': nrm(ks[26], (L, D_FF, D_MODEL), D_FF ** -0.5),
    }

def reference(x_prompt, x_sample, cache_k, cache_v, state_ssm_re, state_ssm_im,
              attn_norm_g, w_in, q_norm_g, k_norm_g, attn_sinks,
              ssm_A_re, ssm_A_im, ssm_log_dt, ssm_B_re, ssm_B_im, ssm_C_re, ssm_C_im, ssm_D,
              w_glu, b_glu, attn_out_g, ssm_out_g, w_out, mlp_norm_g, w_mlp_up, w_mlp_down):
    xp = x_prompt
    xs = x_sample
    zeros_state = jnp.zeros((x_prompt.shape[0], N_SSM_GROUPS, STATE_DIM), jnp.float32)
    nkp, nvp, nrp, nip = [], [], [], []
    nks, nvs, nrs, nis = [], [], [], []
    for l in range(DEPTH):
        p = dict(attn_norm_g=attn_norm_g[l], w_in=w_in[l], q_norm_g=q_norm_g[l],
                 k_norm_g=k_norm_g[l], attn_sinks=attn_sinks[l],
                 ssm_A_re=ssm_A_re[l], ssm_A_im=ssm_A_im[l], ssm_log_dt=ssm_log_dt[l],
                 ssm_B_re=ssm_B_re[l], ssm_B_im=ssm_B_im[l],
                 ssm_C_re=ssm_C_re[l], ssm_C_im=ssm_C_im[l], ssm_D=ssm_D[l],
                 w_glu=w_glu[l], b_glu=b_glu[l], attn_out_g=attn_out_g[l],
                 ssm_out_g=ssm_out_g[l], w_out=w_out[l], mlp_norm_g=mlp_norm_g[l],
                 w_mlp_up=w_mlp_up[l], w_mlp_down=w_mlp_down[l])
        xp, kp, vp, hrp, hip = hybrid_layer(xp, None, None, zeros_state, zeros_state, p)
        xs, ks_, vs_, hrs, his = hybrid_layer(xs, cache_k[l], cache_v[l],
                                              state_ssm_re[l], state_ssm_im[l], p)
        nkp.append(kp); nvp.append(vp); nrp.append(hrp); nip.append(hip)
        nks.append(ks_); nvs.append(vs_); nrs.append(hrs); nis.append(his)
    return (xp, xs,
            jnp.stack(nkp), jnp.stack(nvp), jnp.stack(nrp), jnp.stack(nip),
            jnp.stack(nks), jnp.stack(nvs), jnp.stack(nrs), jnp.stack(nis))


_drawn_inputs = setup_inputs


def setup_inputs(seed=0):
    import zlib

    import numpy as np

    out = dict(_drawn_inputs(seed))
    spreads = {}
    factors = {'q_norm_g': 2.949, 'ssm_A_re': 18.937, 'b_glu': 24.761}
    for name, (base, spread) in spreads.items():
        noise = np.random.default_rng([zlib.crc32(name.encode()), seed]).standard_normal(out[name].shape)
        drawn = base * np.exp(spread * noise) if base else spread * noise
        out[name] = __import__('jax').numpy.asarray(drawn.astype(out[name].dtype))
    for name, factor in factors.items():
        out[name] = (out[name] * factor).astype(out[name].dtype)
    return out
```

```python
from contextlib import ExitStack

import concourse.bass as bass
import numpy as np
from concourse import mybir

F32 = mybir.dt.float32
F32R = mybir.dt.float32r
ALU = mybir.AluOpType
ACT = mybir.ActivationFunctionType
AX = mybir.AxisListType

D_MODEL, SEQ, DEC_BATCH, DEC_SEQ = 2048, 256, 8, 4
ATTN_WIDTH = SSM_WIDTH = D_MODEL // 2
HEAD_DIM, N_KV_HEADS, Q_PER_KV, WINDOW = 64, 4, 4, 128
N_HEADS = N_KV_HEADS * Q_PER_KV
KV_WIDTH = N_KV_HEADS * HEAD_DIM
SSM_GROUP, STATE_DIM = 16, 64
N_GROUPS = SSM_WIDTH // SSM_GROUP
D_FF = 4 * D_MODEL
EPS = 1e-6
P = 128
SAMPLE = DEC_BATCH * DEC_SEQ
TOK = SEQ + SAMPLE
KT = D_MODEL // P
QT = ATTN_WIDTH // P
PAIRS = N_GROUPS // 2
CHUNK = 16
NCHUNK = SEQ // CHUNK
MASKED = -1e30

STEP_K, STEP_N = 2, 512
STEP_COLS = STEP_K * STEP_N
OUTS = STEP_N // P
SLOTS = 4
GROUP_STEPS = KT // STEP_K
HALF_STEPS = GROUP_STEPS // 2
S_U0, S_KV, S_U1, S_Q0, S_Q1 = 0, 8, 16, 24, 32
S_WA = 40
S_GLU = S_WA + 4 * HALF_STEPS
S_WS = S_GLU + 2 * HALF_STEPS
S_MLP = S_WS + 4 * HALF_STEPS
N_BLOCKS = 4
BLOCK_STEPS = 8 * GROUP_STEPS
N_STEPS = S_MLP + N_BLOCKS * BLOCK_STEPS
POOL_SPLITS = range(12, S_WA + 16)

UNITS = (
    [("g_u0", 1), ("rms_x", 1), ("none", 0), ("b_turn", 1)]
    + [(f"bu0_{k}", 1) for k in range(8)]
    + [("g_kv", 1), ("g_u1", 1), ("kv_aux", 3), ("g_q0", 1), ("none", 0), ("g_q1", 1), ("qn0", 1),
       ("qn1", 1), ("sc0", 1), ("ssc", 1), ("y0", 1)]
    + [(f"bu1_{k}", 1) for k in range(8)]
    + [("pt0", 1), ("sc1", 1), ("spt", 2), ("pt1", 1), ("sc2", 1), ("pv0", 2), ("spv", 1), ("pt2", 1),
       ("sc3", 1), ("pt3", 1), ("none", 0), ("pv1", 2), ("wa0", 1), ("rms_a", 1), ("wa1", 1), ("wa2", 1), ("wa3", 1), ("y1", 1),
       ("glu0", 1), ("glu1", 1), ("ws0", 1), ("rms_s", 1), ("ws1", 1), ("ws2", 1), ("ws3", 1),
       ("up0", 1), ("up1", 1), ("rms_h", 1), ("up2", 1), ("up3", 1)]
)
UNIT = {name: i for i, (name, _) in enumerate(UNITS)}
N_UNITS = len(UNITS)


STEPS_AT_END = {"g_u0": S_KV, "g_kv": S_U1, "g_u1": S_Q0, "g_q0": S_Q1, "g_q1": S_WA}
for _g in range(4):
    STEPS_AT_END[f"wa{_g}"] = S_WA + HALF_STEPS * (_g + 1)
    STEPS_AT_END[f"ws{_g}"] = S_WS + HALF_STEPS * (_g + 1)
    STEPS_AT_END[f"up{_g}"] = S_MLP + GROUP_STEPS * (_g + 1)
    if _g < 2:
        STEPS_AT_END[f"glu{_g}"] = S_GLU + HALF_STEPS * (_g + 1)


def steps_at_end(unit):
    if unit < N_UNITS:
        return STEPS_AT_END.get(UNITS[unit][0])
    return S_MLP + GROUP_STEPS * (4 + unit - N_UNITS + 1)


def small_units(unit):
    return sum(name not in STEPS_AT_END and name != "none" for name, _ in UNITS[:unit + 1])


def evacuations(unit):
    return sum(n for _, n in UNITS[unit % 2:unit + 1:2]) + len(
        range(N_UNITS + (unit - N_UNITS) % 2, unit + 1, 2))


SMALL = {}


def _small_columns():
    at = 0
    for name, width in (("g_in", KT), ("g_mlp", KT), ("g_attn", QT), ("g_ssm", QT), ("d_skip", QT),
                        ("b_glu", QT), ("g_q", 1), ("g_k", 1), ("sink_rows", 2),
                        ("sinks", N_HEADS), ("a_re", PAIRS), ("a_im", PAIRS), ("log_dt", PAIRS),
                        ("h0", 2 * PAIRS * DEC_BATCH), ("eps", 1)):
        SMALL[name] = slice(at, at + width)
        at += width
    return at


N_SMALL = _small_columns()
CONST = {"ident": slice(0, 128), "ones": slice(128, 256), "head_mean": slice(256, 384),
         "delta": slice(384, 768)}
N_CONST = 768
SAMPLE_KEYS = WINDOW + SAMPLE
ACROSS_BEFORE_Q1 = 16
SLOPES = [2.0 ** (-8.0 * (h + 1) / N_HEADS) for h in range(N_HEADS)]


def build_program(nc, ins, outs):
    ctx = ExitStack()
    with ctx:
        place = [16512]

        def sb(name, cols, dt=F32, at=None):
            if at is None:
                at = place[0]
                place[0] += -(-4 * cols // 32) * 32
                assert place[0] <= 229344, place[0]
            return nc.alloc_sbuf_tensor_at(name, [P, cols], dt, offset=at), at

        def sem(name):
            return ctx.enter_context(nc.semaphore(name))

        T4 = OUTS * TOK
        w_raw, _ = sb("w_raw", SLOTS * STEP_COLS)
        w_hi, _ = sb("w_hi", SLOTS * STEP_COLS, F32R)
        w_lo, _ = sb("w_lo", SLOTS * STEP_COLS, F32R)
        h_t, _ = sb("h_t", KT * TOK)
        mov_a, at_a = sb("mov_a", KT * 2 * TOK, F32R)
        mov_b, at_b = sb("mov_b", KT * 2 * TOK, F32R)
        u_t, at_u = sb("u_t", QT * TOK)
        q_t, at_q = sb("q_t", QT * TOK)
        kv_t, _ = sb("kv_t", T4)
        v_tok, _ = sb("v_tok", 3 * KV_WIDTH)
        c_w, at_c = sb("c_w", 2 * PAIRS * 32)
        b_w, at_bw = sb("b_w", 2 * QT * P)
        powers, _ = sb("powers", 3 * PAIRS * CHUNK)
        t_1, at_t1 = sb("t_1", 2 * 16 * CHUNK)
        t_2, _ = sb("t_2", 2 * 16 * CHUNK)
        sq, at_sq = sb("sq", T4)
        au, _ = sb("au", T4)
        small, _ = sb("small", N_SMALL)
        const, _ = sb("const", N_CONST)
        r_b, _ = sb("r_b", TOK)
        ssq, _ = sb("ssq", TOK)
        stat, _ = sb("stat", 49)
        last_0, _ = sb("last_0", 2 * 16 * 9)
        x_g, _ = sb("x_g", KT * TOK, at=at_b)
        x_sq, _ = sb("x_sq", KT * TOK, at=at_b + 4 * KT * TOK)
        b_nat, _ = sb("b_nat", 2 * 1024, at=at_q)
        b_bar, _ = sb("b_bar", 2 * 1024, at=at_c)
        states, _ = sb("states", 2 * 16 * TOK, at=at_b)
        v_cache, _ = sb("v_cache", DEC_BATCH * KV_WIDTH, at=at_bw)
        a_hi_end = at_a + 4 * QT * 2 * TOK
        k_cache, _ = sb("k_cache", 2 * DEC_BATCH * WINDOW, at=at_a)
        s_samp, _ = sb("s_samp", 4 * 160, at=at_a + 8192)
        pt_samp, _ = sb("pt_samp", 512, at=at_a + 8192 + 2560)
        pt_new, _ = sb("pt_new", 512, at=at_a + 8192 + 2560 + 2048)
        at_bias = at_a + 8192 + 2560 + 2048 + 2048
        sample_bias, _ = sb("sample_bias", 4 * SAMPLE_KEYS, at=at_bias)
        samp_o, _ = sb("samp_o", 2 * P, at=at_bias + 2560)
        q_blk, _ = sb("q_blk", 2 * DEC_BATCH * 32, at=a_hi_end + 6144 + 6144)
        disc, _ = sb("disc", 14 * PAIRS, at=at_sq)
        ssq_part, _ = sb("ssq_part", TOK, at=at_t1)
        last_1, _ = sb("last_1", 2 * 16 * 9, at=at_bw)
        s_head, _ = sb("s_head", 4 * 384, at=a_hi_end)
        pt_head, _ = sb("pt_head", 2 * 4 * 384, at=a_hi_end + 6144)
        t_b, _ = sb("t_b", 2 * T4, at=at_q)
        s_relu, _ = sb("s_relu", 2 * T4, at=at_u)

        psum = ctx.enter_context(nc.psum_tensor("psum", [P, 8, 512], F32))

        raw3 = w_raw[:, :].rearrange("p (s n) -> p s n", s=SLOTS)
        hi3 = w_hi[:, :].rearrange("p (s n) -> p s n", s=SLOTS)
        lo3 = w_lo[:, :].rearrange("p (s n) -> p s n", s=SLOTS)
        hi4 = w_hi[:, :].rearrange("p (s k n) -> p s k n", s=SLOTS, k=STEP_K)
        lo4 = w_lo[:, :].rearrange("p (s k n) -> p s k n", s=SLOTS, k=STEP_K)
        h3 = h_t[:, :].rearrange("p (k t) -> p k t", t=TOK)
        a4 = mov_a[:, :].rearrange("p (k h t) -> p k h t", h=2, t=TOK)
        b4 = mov_b[:, :].rearrange("p (k h t) -> p k h t", h=2, t=TOK)
        xg3 = x_g[:, :].rearrange("p (k t) -> p k t", t=TOK)
        xsq3 = x_sq[:, :].rearrange("p (k t) -> p k t", t=TOK)
        u3 = u_t[:, :].rearrange("p (k t) -> p k t", t=TOK)
        q3 = q_t[:, :].rearrange("p (k t) -> p k t", t=TOK)
        kv3 = kv_t[:, :].rearrange("p (k t) -> p k t", t=TOK)
        v3 = v_tok[:, :].rearrange("p (k c) -> p k c", c=KV_WIDTH)
        c4 = c_w[:, :].rearrange("p (r j c) -> p r j c", r=2, c=32)
        bbar4 = b_bar[:, :].rearrange("p (r j c) -> p r j c", r=2, c=32)
        bnat4 = b_nat[:, :].rearrange("p (r j c) -> p r j c", r=2, c=32)
        bw4 = b_w[:, :].rearrange("p (r q m) -> p r q m", r=2, m=P)
        pw4 = powers[:, :].rearrange("p (r j s) -> p r j s", r=3, s=CHUNK)
        t1v = t_1[:, :].rearrange("p (r j s) -> p r j s", r=2, s=CHUNK)
        t2v = t_2[:, :].rearrange("p (r j s) -> p r j s", r=2, s=CHUNK)
        sq3 = sq[:, :].rearrange("p (k t) -> p k t", t=TOK)
        au3 = au[:, :].rearrange("p (k t) -> p k t", t=TOK)
        st4 = states[:, :].rearrange("p (r j t) -> p r j t", r=2, t=TOK)
        h0v = small[:, SMALL["h0"]].rearrange("p (r j n) -> p r j n", r=2, n=DEC_BATCH)
        vc3 = v_cache[:, :].rearrange("p (n c) -> p n c", n=DEC_BATCH)
        kc4 = k_cache[:, :].rearrange("p (g n s) -> p g n s", g=2, s=WINDOW)
        ss3 = s_samp[:, :].rearrange("p (b s) -> p b s", b=4)
        pts = pt_samp[:, :].rearrange("p (g n h c) -> p g n h c", g=2, n=DEC_BATCH, h=2)
        ptn = pt_new[:, :].rearrange("p (g n h c) -> p g n h c", g=2, n=DEC_BATCH, h=2)
        sh3 = s_head[:, :].rearrange("p (b s) -> p b s", b=4)
        pt4 = pt_head[:, :].rearrange("p (u b s) -> p u b s", u=2, b=4)
        tb4 = t_b[:, :].rearrange("p (u k t) -> p u k t", u=2, t=TOK)
        sr4 = s_relu[:, :].rearrange("p (u k t) -> p u k t", u=2, t=TOK)
        so3 = samp_o[:, :].rearrange("p (g c) -> p g c", g=2)
        qb4 = q_blk[:, :].rearrange("p (g n c) -> p g n c", g=2, n=DEC_BATCH)
        last4 = [t[:, :].rearrange("p (r j n) -> p r j n", r=2, n=9) for t in (last_0, last_1)]
        disc3 = disc[:, :].rearrange("p (k j) -> p k j", j=PAIRS)
        ident = const[:, CONST["ident"]]
        ones = const[:, CONST["ones"]]
        head_mean = const[:, CONST["head_mean"]]
        eps = small[:, SMALL["eps"]]
        DT, AR, TH, TC, K0, K1, MAG, SIN, COS, ABR, ABI, CR, CI, TMP = range(14)

        def gain(name, tiles, width=TOK):
            at = SMALL[name]
            return small[:, at.start + tiles.start:at.start + tiles.stop].unsqueeze(2) \
                .to_broadcast([P, tiles.stop - tiles.start, width])

        def over_tiles(ap, n):
            return ap.unsqueeze(1).to_broadcast([P, n, TOK])

        def banks(unit, n=OUTS, cols=TOK):
            b = 4 * (unit % 2)
            return psum[:, b:b + n, 0:cols]

        raw_loaded = [sem(f"raw_loaded{i}") for i in range(SLOTS)]
        x_loaded = [sem(f"x_loaded{i}") for i in range(4)]
        small_loaded = sem("small_loaded")
        const_loaded = sem("const_loaded")
        b_loaded = sem("b_loaded")
        c_loaded = sem("c_loaded")
        kc_loaded = sem("kc_loaded")
        bias_loaded = sem("bias_loaded")
        vc_loaded = sem("vc_loaded")
        stored = sem("stored")
        hi_split = sem("hi_split")
        lo_split = [sem(f"lo_split{i}") for i in range(SLOTS)]
        step_used = sem("step_used")
        psum_full = sem("psum_full")
        evacuated = [sem("evacuated_even"), sem("evacuated_odd")]
        dve_done = sem("dve_done")
        act_done = sem("act_done")
        pool_done = sem("pool_done")
        x_gained = sem("x_gained")
        x_hi = sem("x_hi")
        x_lo = sem("x_lo")
        x_squared = sem("x_squared")
        x_summed = sem("x_summed")
        rms_root = sem("rms_root")
        disc_arg = sem("disc_arg")
        disc_fun = sem("disc_fun")
        disc_ready = sem("disc_ready")
        bbar_ready = sem("bbar_ready")
        powers_ready = sem("powers_ready")
        c_ready = sem("c_ready")
        squared = sem("squared")
        rsqrt_ready = sem("rsqrt_ready")
        k_ready = sem("k_ready")
        q_ready = sem("q_ready")
        qblk_ready = sem("qblk_ready")
        scanned = sem("scanned")
        max_ready = sem("max_ready")
        exp_ready = sem("exp_ready")
        sum_inverted = sem("sum_inverted")
        probs_ready = sem("probs_ready")
        mix_raw = sem("mix_raw")
        mix_squared = sem("mix_squared")
        mix_gained = sem("mix_gained")
        mix_hi = sem("mix_hi")
        mix_lo = sem("mix_lo")
        mix_summed = sem("mix_summed")
        gelu_ready = sem("gelu_ready")
        g_hi = sem("g_hi")
        g_lo = sem("g_lo")
        r_ready = sem("r_ready")
        added = sem("added")
        h_gained = sem("h_gained")
        h_hi = sem("h_hi")
        h_lo = sem("h_lo")
        h_squared = sem("h_squared")
        h_summed = sem("h_summed")
        hid_ready = sem("hid_ready")
        hid_hi = sem("hid_hi")
        hid_lo = sem("hid_lo")
        last_copied = sem("last_copied")
        q_blk_zero = sem("q_blk_zero")

        block = ctx.enter_context(nc.Block())

        def unit_free(pe, unit, past=0):
            if unit >= 2:
                pe.wait_ge(evacuated[unit % 2], past * 4 + evacuations(unit - 2))

        def unit_full(eng, unit, past=0):
            steps = steps_at_end(unit)
            if steps is None:
                eng.wait_ge(psum_full, small_units(unit))
            else:
                eng.wait_ge(step_used, past * BLOCK_STEPS + steps)

        def unit_read(eng, unit, past=0):
            eng.wait_ge(evacuated[unit % 2], past * 4 + evacuations(unit))

        @block.sync
        def _(sp):
            def load_step(n):
                if n >= SLOTS:
                    sp.wait_ge(lo_split[n % SLOTS], n // SLOTS)
                sp.dma_start(raw3[:, n % SLOTS, :], ins["w"][n, :, :]).then_inc(raw_loaded[n % SLOTS], 16)

            sp.dma_start(small[:, :], ins["small"][:, :]).then_inc(small_loaded, 16)
            for k in range(4):
                sp.dma_start(h_t[:, k * T4:(k + 1) * T4], ins["x"][:, k * T4:(k + 1) * T4]) \
                    .then_inc(x_loaded[k], 16)
                if k == 0:
                    load_step(0)
            load_step(1)
            sp.dma_start(b_nat[:, :], ins["b"][:, :]).then_inc(b_loaded, 16)
            sp.dma_start(const[:, :], ins["const"][:, :]).then_inc(const_loaded, 16)
            for n in range(2, S_U1):
                load_step(n)
            unit_full(sp, UNIT["b_turn"])
            sp.dma_start(c_w[:, :], ins["c"][:, :]).then_inc(c_loaded, 16)
            for n in range(S_U1, S_WA):
                load_step(n)
            for n in range(S_WA, S_WA + SLOTS):
                load_step(n)
            unit_full(sp, UNIT["g_q1"])
            sp.dma_start(k_cache[:, :], ins["kc"][:, :]).then_inc(kc_loaded, 16)
            sp.dma_start(sample_bias[:, :], ins["sample_bias"][:, :]).then_inc(bias_loaded, 16)
            unit_full(sp, UNIT["bu1_7"])
            sp.dma_start(vc3, ins["vc"].rearrange("n s c -> s n c")).then_inc(vc_loaded, 16)
            sp.wait_ge(k_ready, 1)
            sp.dma_start(outs["kv"][:, :], kv_t[:, :]).then_inc(stored, 16)
            sp.dma_start(outs["kc"][:, :, :, :],
                         ins["kc"].rearrange("p (g n s) -> p g n s", g=2, s=WINDOW)[:, :, :, DEC_SEQ:WINDOW]) \
                .then_inc(stored, 16)
            sp.dma_start(outs["vc"][:, :, :], ins["vc"][:, DEC_SEQ:WINDOW, :]).then_inc(stored, 16)
            for n in range(S_WA + SLOTS, S_MLP):
                load_step(n)
            with sp.Fori(0, (N_STEPS - S_MLP) // SLOTS) as i:
                for s in range(SLOTS):
                    sp.wait_ge(lo_split[s], i + S_MLP // SLOTS)
                    sp.dma_start(raw3[:, s, :],
                                 ins["w"][bass.ds(i * SLOTS + (S_MLP + s), 1), :, :].rearrange("o p n -> p (o n)")) \
                        .then_inc(raw_loaded[s], 16)
            for half, kept in enumerate((last_0, last_1)):
                sp.wait_ge(last_copied, half + 1)
                sp.dma_start(outs["last"][half, :, :], kept[:, :]).then_inc(stored, 16)
            for g in range(4):
                sp.wait_ge(added, 8 + 4 * (N_BLOCKS - 1) + g + 1)
                sp.dma_start(outs["y"][:, g * T4:(g + 1) * T4], h_t[:, g * T4:(g + 1) * T4]) \
                    .then_inc(stored, 16)
            sp.wait_ge(stored, 16 * (5 + 4))

        @block.scalar
        def _(act):
            def hi_part(n, past=0):
                act.wait_ge(raw_loaded[n % SLOTS], past * (16 * BLOCK_STEPS // SLOTS) + (n // SLOTS + 1) * 16)
                if n >= SLOTS:
                    act.wait_ge(step_used, past * BLOCK_STEPS + n - SLOTS + 1)
                nc.scalar.activation(hi3[:, n % SLOTS, :], raw3[:, n % SLOTS, :], ACT.Copy) \
                    .then_inc(hi_split, 1)

            def hi_parts(steps, past=0):
                for n in steps:
                    hi_part(n, past)

            act.wait_ge(small_loaded, 16)
            nc.scalar.activation(disc3[:, DT, :], small[:, SMALL["log_dt"]], ACT.Exp).then_inc(disc_fun, 1)
            act.wait_ge(disc_arg, 1)
            nc.scalar.activation(disc3[:, MAG, :], disc3[:, AR, :], ACT.Exp).then_inc(disc_fun, 1)
            nc.scalar.activation(disc[:, SIN * PAIRS:(COS + 1) * PAIRS],
                                 disc[:, TH * PAIRS:(TC + 1) * PAIRS], ACT.Sin).then_inc(disc_fun, 1)
            for k in range(4):
                act.wait_ge(x_gained, k + 1)
                nc.scalar.activation(a4[:, 4 * k:4 * k + 4, 0, :], xg3[:, 4 * k:4 * k + 4, :], ACT.Copy) \
                    .then_inc(x_hi, 1)
                hi_part(k)
            nc.scalar.activation(x_sq[:, :], h_t[:, :], ACT.Square).then_inc(x_squared, 1)

            def root(unit, mean):
                unit_full(act, unit)
                nc.scalar.activation(r_b[:, :], banks(unit, 1)[:, 0, :], ACT.Sqrt, bias=eps, scale=mean) \
                    .then_inc(evacuated[unit % 2], 1)

            hi_parts(range(4, 10))
            root(UNIT["rms_x"], 1.0 / D_MODEL)
            u = UNIT["b_turn"]
            unit_full(act, u)
            nc.scalar.activation(b_w[:, :].rearrange("p (b n) -> p b n", b=4), banks(u, 4, 512), ACT.Copy) \
                .then_inc(evacuated[u % 2], 1)
            hi_parts(range(10, 12))

            def bu_out(half):
                for k in range(0, 8, 2):
                    u = UNIT[f"bu{half}_{k}"]
                    unit_full(act, u)
                    nc.scalar.activation(st4[:, :, 2 * k:2 * k + 2, :].rearrange("p r j t -> p j r t"),
                                         banks(u).rearrange("p (j r) t -> p j r t", r=2), ACT.Copy) \
                        .then_inc(evacuated[u % 2], 1)

            act.wait_ge(powers_ready, 1)
            act.wait_ge(x_summed, 1)
            bu_out(0)
            hi_parts(range(12, 20))
            unit_read(act, UNIT["g_kv"])
            nc.scalar.activation(sq3[:, 0:2, :], kv3[:, 0:2, :], ACT.Square).then_inc(squared, 1)
            hi_parts(range(20, 28))
            act.wait_ge(c_loaded, 16)
            nc.scalar.mul(c4[:, 1, :, :], c4[:, 1, :, :], -1.0).then_inc(c_ready, 1)

            def head_scale(unit, dst, n):
                unit_full(act, unit)
                nc.scalar.activation(dst, banks(unit, n), ACT.Ln, bias=eps).then_inc(evacuated[unit % 2], 1)

            u = UNIT["kv_aux"]
            head_scale(u, sq3[:, 0:2, :], 2)
            b0 = 4 * (u % 2)
            nc.scalar.activation(v_tok[:, 0:512], psum[:, b0 + 2, 0:512], ACT.Copy).then_inc(evacuated[u % 2], 1)
            nc.scalar.activation(v_tok[0:SAMPLE, 512:768], psum[0:SAMPLE, b0 + 3, 0:256], ACT.Copy) \
                .then_inc(evacuated[u % 2], 1)
            unit_read(act, u)
            nc.scalar.activation(sq3[:, 0:2, :], sq3[:, 0:2, :], ACT.Exp, scale=-0.5).then_inc(rsqrt_ready, 1)
            hi_parts(range(28, 36))
            unit_read(act, UNIT["g_q0"])
            act.wait_ge(k_ready, 1)
            nc.scalar.activation(sq3, q3[:, 0:4, :], ACT.Square).then_inc(squared, 1)
            hi_parts(range(36, 40))
            head_scale(UNIT["qn0"], sq3, 4)
            unit_read(act, UNIT["qn0"])
            nc.scalar.activation(sq3, sq3, ACT.Exp, scale=-0.5).then_inc(rsqrt_ready, 1)
            hi_parts(range(40, 44))
            unit_read(act, UNIT["g_q1"])
            nc.scalar.activation(au3, q3[:, 4:8, :], ACT.Square).then_inc(squared, 1)
            head_scale(UNIT["qn1"], au3, 4)
            unit_read(act, UNIT["qn1"])
            nc.scalar.activation(au3, au3, ACT.Exp, scale=-0.5).then_inc(rsqrt_ready, 1)

            def exps(i):
                act.wait_ge(max_ready, i + 1)
                if i == 1:
                    for b in range(4):
                        nc.scalar.activation(ss3[:, b, :], ss3[:, b, :], ACT.Exp, bias=stat[:, 36 + b:37 + b],
                                             accum_out=stat[:, 40 + b:41 + b])
                    nc.scalar.activation(stat[:, 44:48], stat[:, 44:48], ACT.Exp).then_inc(exp_ready, 1)
                    return
                for blk, cols in ((0, slice(0, 128)), (1, slice(128, 384))):
                    for b in range(4):
                        nc.scalar.activation(sh3[:, b, cols], sh3[:, b, cols], ACT.Exp,
                                             bias=stat[:, 8 + 4 * blk + b:9 + 4 * blk + b],
                                             accum_out=stat[:, 16 + 4 * blk + b:17 + 4 * blk + b])
                nc.scalar.activation(stat[:, 24:32], stat[:, 24:32], ACT.Exp).then_inc(exp_ready, 1)

            def soft_scale(n_softmax):
                act.wait_ge(sum_inverted, n_softmax + 1)
                if n_softmax == 1:
                    for b in range(4):
                        scaled = nc.scalar.activation(ss3[:, b, :], ss3[:, b, :], ACT.Copy,
                                                      scale=stat[:, 40 + b:41 + b])
                    scaled.then_inc(probs_ready, 1)
                    return
                for blk, cols in ((0, slice(0, 128)), (1, slice(128, 384))):
                    for b in range(4):
                        at = 16 + 4 * blk + b
                        scaled = nc.scalar.activation(sh3[:, b, cols], sh3[:, b, cols], ACT.Copy,
                                                      scale=stat[:, at:at + 1])
                scaled.then_inc(probs_ready, 1)

            def pt_out(i):
                u = UNIT[f"pt{i}"]
                unit_full(act, u)
                if i >= 2 and i % 2 == 0:
                    unit_full(act, UNIT["pv0"])
                nc.scalar.activation(pt4[:, i % 2, :, :], banks(u, 4, 384), ACT.Copy) \
                    .then_inc(evacuated[u % 2], 1)

            def attention_squares(g):
                u = UNIT[f"pv{g}"]
                unit_full(act, u)
                act.wait_ge(mix_summed, g) if g else act.wait_ge(q_ready, 1)
                nc.scalar.activation(sq3[:, :, 0:SEQ], banks(u, 4, SEQ), ACT.Square).then_inc(evacuated[u % 2], 1)
                unit_read(act, UNIT["spv"])
                nc.scalar.activation(sq3[:, :, SEQ:TOK].rearrange("p r (n i) -> p r n i", i=DEC_SEQ),
                                     so3[:, g, :].rearrange("p (n r i) -> p r n i", r=Q_PER_KV, i=DEC_SEQ),
                                     ACT.Square).then_inc(mix_squared, 1)

            def attention_hi(g):
                act.wait_ge(mix_gained, g + 1)
                nc.scalar.activation(a4[:, 4 * g:4 * g + 4, 0, :], au3, ACT.Copy).then_inc(mix_hi, 1)

            def ssm_parts(m, dst):
                act.wait_ge(mix_raw, m - 1)
                act.wait_ge(mix_summed, m)
                nc.scalar.activation(sq3, au3, ACT.Square).then_inc(mix_squared, 1)
                act.wait_ge(mix_gained, m + 1)
                if m == 2:
                    act.wait_ge(last_copied, 2)
                nc.scalar.activation(dst, au3, ACT.Copy).then_inc(mix_hi, 1)

            exps(0)
            exps(1)
            unit_full(act, UNIT["y0"])
            act.wait_ge(last_copied, 1)
            bu_out(1)
            soft_scale(0)
            soft_scale(1)
            pt_out(0)
            exps(2)
            u = UNIT["spt"]
            unit_full(act, u)
            b0 = 4 * (u % 2)
            nc.scalar.activation(pt_samp[:, :], psum[:, b0, 0:512], ACT.Copy).then_inc(evacuated[u % 2], 1)
            nc.scalar.activation(pt_new[0:SAMPLE, :], psum[0:SAMPLE, b0 + 1, 0:512], ACT.Copy) \
                .then_inc(evacuated[u % 2], 1)
            soft_scale(2)
            pt_out(1)
            exps(3)
            u = UNIT["spv"]
            unit_full(act, u)
            nc.scalar.activation(so3, psum[:, 4 * (u % 2):4 * (u % 2) + 2, 0:P], ACT.Copy) \
                .then_inc(evacuated[u % 2], 1)
            attention_squares(0)
            soft_scale(3)
            attention_hi(0)
            pt_out(2)
            exps(4)
            soft_scale(4)
            pt_out(3)
            attention_squares(1)
            attention_hi(1)
            hi_parts(range(44, 48))
            root(UNIT["rms_a"], 1.0 / ATTN_WIDTH)
            hi_parts(range(48, 56))
            unit_read(act, UNIT["y0"])
            nc.scalar.activation(u3[:, 0:4, :], u3[:, 0:4, :], ACT.Gelu_apprx_tanh).then_inc(gelu_ready, 1)
            hi_parts(range(56, 60))
            unit_read(act, UNIT["y1"])
            nc.scalar.activation(u3[:, 4:8, :], u3[:, 4:8, :], ACT.Gelu_apprx_tanh).then_inc(gelu_ready, 1)
            for m in range(2):
                act.wait_ge(gelu_ready, m + 1)
                nc.scalar.activation(a4[:, 8 + 4 * m:12 + 4 * m, 0, :], u3[:, 4 * m:4 * m + 4, :], ACT.Copy) \
                    .then_inc(g_hi, 1)
            for m in range(2):
                hi_parts(range(60 + 4 * m, 64 + 4 * m))
                u = UNIT[f"glu{m}"]
                unit_full(act, u)
                if m == 0:
                    act.wait_ge(added, 4)
                for o in range(4):
                    at = SMALL["b_glu"].start + 4 * m + o
                    gate = nc.scalar.activation(tb4[:, m, o, :], banks(u)[:, o, :], ACT.Sigmoid,
                                                bias=small[:, at:at + 1])
                gate.then_inc(evacuated[u % 2], 1)
                ssm_parts(2 + m, b4[:, 4 * m:4 * m + 4, 0, :])
            hi_parts(range(68, 72))
            root(UNIT["rms_s"], 1.0 / SSM_WIDTH)

            def h_parts(g):
                act.wait_ge(added, 4 + g + 1)
                act.wait_ge(h_summed, g) if g else act.wait_ge(mix_summed, 4)
                nc.scalar.activation(sq3, h3[:, 4 * g:4 * g + 4, :], ACT.Square).then_inc(h_squared, 1)
                act.wait_ge(h_gained, g + 1)
                nc.scalar.activation(a4[:, 4 * g:4 * g + 4, 0, :], au3, ACT.Copy).then_inc(h_hi, 1)

            for g in range(4):
                if g:
                    hi_parts(range(68 + 4 * g, 72 + 4 * g))
                h_parts(g)

            def mlp_hi(group, past=0, last=False):
                n = S_MLP + GROUP_STEPS * group + SLOTS
                hi_parts(range(n, n + GROUP_STEPS - (SLOTS if last else 0)), past)

            def relu_part(g, past=0, before=0):
                act.wait_ge(hid_ready, past * 4 + (before + g + 1))
                nc.scalar.activation(b4[:, 4 * g:4 * g + 4, 0, :], sr4[:, g % 2, :, :], ACT.Copy) \
                    .then_inc(hid_hi, 1)

            for g in range(4):
                mlp_hi(g)
                relu_part(g)
                if g == 1:
                    root(UNIT["rms_h"], 1.0 / D_MODEL)
            with act.Fori(0, N_BLOCKS - 1) as b:
                for g in range(4):
                    mlp_hi(4 + g, b)
                for g in range(4):
                    mlp_hi(8 + g, b)
                    relu_part(g, b, before=4)
            for g in range(4):
                mlp_hi(4 + g, N_BLOCKS - 1, last=g == 3)

        @block.vector
        def _(dve):
            own = [0]

            def link(ins_):
                own[0] += 1
                ins_.then_inc(dve_done, 1)

            def linked():
                dve.wait_ge(dve_done, own[0])

            def lo_part(n, past=0):
                if n in POOL_SPLITS:
                    return
                dve.wait_ge(hi_split, past * BLOCK_STEPS + n + 1)
                nc.vector.tensor_tensor(lo3[:, n % SLOTS, :], raw3[:, n % SLOTS, :],
                                        hi3[:, n % SLOTS, :].bitcast(F32), ALU.subtract) \
                    .then_inc(lo_split[n % SLOTS], 1)

            def lo_parts(steps, past=0):
                for n in steps:
                    lo_part(n, past)

            def tt(out, x, y, op):
                return nc.vector.tensor_tensor(out, x, y, op)

            dve.wait_ge(disc_fun, 1)
            a_re, a_im = small[:, SMALL["a_re"]], small[:, SMALL["a_im"]]
            two_pi, whole = 2 * np.pi, 1.5 * 2.0 ** 23
            pi_hi = 6.28125
            both = disc[:, TH * PAIRS:(TC + 1) * PAIRS]
            turns = disc[:, K0 * PAIRS:(K1 + 1) * PAIRS]
            link(tt(disc3[:, AR, :], a_re, disc3[:, DT, :], ALU.mult))
            link(tt(disc3[:, TH, :], a_im, disc3[:, DT, :], ALU.mult))
            linked()
            link(nc.vector.tensor_scalar(disc3[:, TC, :], disc3[:, TH, :], np.pi / 2, None, ALU.add))
            linked()
            link(nc.vector.tensor_scalar(turns, both, 1 / two_pi, whole, ALU.mult, ALU.add))
            linked()
            link(nc.vector.tensor_scalar(turns, turns, -whole, None, ALU.add))
            linked()
            link(nc.vector.scalar_tensor_tensor(both, turns, -pi_hi, both, ALU.mult, ALU.add))
            linked()
            link(nc.vector.scalar_tensor_tensor(both, turns, pi_hi - two_pi, both, ALU.mult, ALU.add))
            linked()
            nc.vector.tensor_scalar(both, both, 3.1415925, -3.1415925, ALU.min, ALU.max).then_inc(disc_arg, 1)
            inv, tmp = disc3[:, K0, :], disc3[:, K1, :]
            link(tt(inv, a_re, a_re, ALU.mult))
            link(tt(tmp, a_im, a_im, ALU.mult))
            linked()
            link(tt(inv, inv, tmp, ALU.add))
            linked()
            link(nc.vector.reciprocal(inv, inv))
            dve.wait_ge(disc_fun, 3)
            abr, abi, cr, ci, am1 = (disc3[:, k, :] for k in (ABR, ABI, CR, CI, TMP))
            link(tt(abr, disc3[:, MAG, :], disc3[:, COS, :], ALU.mult))
            link(tt(abi, disc3[:, MAG, :], disc3[:, SIN, :], ALU.mult))
            linked()
            link(nc.vector.tensor_scalar(am1, abr, -1.0, None, ALU.add))
            linked()
            link(tt(cr, am1, a_re, ALU.mult))
            link(tt(tmp, abi, a_im, ALU.mult))
            linked()
            link(tt(cr, cr, tmp, ALU.add))
            linked()
            link(tt(ci, abi, a_re, ALU.mult))
            link(tt(tmp, am1, a_im, ALU.mult))
            linked()
            link(tt(ci, ci, tmp, ALU.subtract))
            linked()
            link(tt(cr, cr, inv, ALU.mult))
            tt(ci, ci, inv, ALU.mult).then_inc(disc_ready, 1)

            def gain_x(k):
                dve.wait_ge(x_loaded[k], 16)
                tt(xg3[:, 4 * k:4 * k + 4, :], h3[:, 4 * k:4 * k + 4, :], gain("g_in", slice(4 * k, 4 * k + 4)),
                   ALU.mult).then_inc(x_gained, 1)

            def lo_x(k):
                dve.wait_ge(x_hi, k + 1)
                tt(a4[:, 4 * k:4 * k + 4, 1, :], xg3[:, 4 * k:4 * k + 4, :],
                   a4[:, 4 * k:4 * k + 4, 0, :].bitcast(F32), ALU.subtract).then_inc(x_lo, 1)

            gain_x(0)
            for k in range(4):
                if k < 3:
                    gain_x(k + 1)
                lo_x(k)
                lo_part(k)
            dve.wait_ge(x_squared, 1)
            nc.vector.tensor_reduce(ssq[:, :], xsq3.rearrange("p k t -> p t k"), AX.X, ALU.add).then_inc(x_summed, 1)
            lo_parts(range(4, 12))

            roots = [0]

            def one_over_root(unit):
                unit_read(dve, unit)
                roots[0] += 1
                nc.vector.reciprocal(r_b[:, :], r_b[:, :]).then_inc(r_ready, 1)
                dve.wait_ge(r_ready, roots[0])

            def project_out(name, dst):
                u = UNIT[name]
                unit_full(dve, u)
                tt(dst, banks(u), over_tiles(r_b[:, :], OUTS), ALU.mult).then_inc(evacuated[u % 2], 1)

            one_over_root(UNIT["rms_x"])
            project_out("g_u0", u3[:, 0:4, :])

            def multiply_add(dst, re, im, src, t1, t2, final=False):
                link(tt(t1, re, src, ALU.mult))
                link(tt(t2, im, src, ALU.mult))
                dve.wait_ge(dve_done, own[0] - 1)
                link(tt(dst, dst, t1, ALU.add))
                linked()
                if final:
                    tt(dst, dst, t2[:, ::-1, :, :], ALU.add).then_inc(scanned, 1)
                    return
                link(tt(dst, dst, t2[:, ::-1, :, :], ALU.add))
                linked()

            a3 = pw4[:, :, :, 0]

            def by_pair(j0, n):
                re = a3[:, 0, j0:j0 + 16].unsqueeze(1).unsqueeze(3).to_broadcast([P, 2, 16, n])
                im = a3[:, 1:3, j0:j0 + 16].unsqueeze(3).to_broadcast([P, 2, 16, n])
                return re, im

            prompt = st4[:, :, :, 0:SEQ].rearrange("p r j (c s) -> p r j c s", s=CHUNK)
            sample = st4[:, :, :, SEQ:TOK].rearrange("p r j (n i) -> p r j n i", i=DEC_SEQ)

            def scan_sample(half):
                re, im = by_pair(16 * half, DEC_BATCH)
                for i in range(DEC_SEQ):
                    src = h0v[:, :, 16 * half:16 * half + 16, :] if i == 0 else sample[:, :, :, :, i - 1]
                    multiply_add(sample[:, :, :, :, i], re, im, src, t1v[:, :, :, 0:DEC_BATCH],
                                 t2v[:, :, :, 0:DEC_BATCH])

            def scan_inside(half, steps):
                re, im = by_pair(16 * half, NCHUNK)
                for s in steps:
                    multiply_add(prompt[:, :, :, :, s], re, im, prompt[:, :, :, :, s - 1], t1v, t2v)

            def scan_across(half, chunks):
                js = slice(16 * half, 16 * half + 16)
                re = pw4[:, 0, js, :].unsqueeze(1).to_broadcast([P, 2, 16, CHUNK])
                im = pw4[:, 1:3, js, :]
                for c in chunks:
                    carry = prompt[:, :, :, c - 1, CHUNK - 1].unsqueeze(3).to_broadcast([P, 2, 16, CHUNK])
                    multiply_add(prompt[:, :, :, c, :], re, im, carry, t1v, t2v, final=c == NCHUNK - 1)

            def bu_out(half):
                for k in range(1, 8, 2):
                    u = UNIT[f"bu{half}_{k}"]
                    unit_full(dve, u)
                    nc.vector.tensor_copy(st4[:, :, 2 * k:2 * k + 2, :].rearrange("p r j t -> p j r t"),
                                          banks(u).rearrange("p (j r) t -> p j r t", r=2)) \
                        .then_inc(evacuated[u % 2], 1)

            def states_there(half):
                unit_read(dve, UNIT[f"bu{half}_6"])
                unit_read(dve, UNIT[f"bu{half}_7"])

            dve.wait_ge(powers_ready, 1)
            bu_out(0)
            states_there(0)
            scan_sample(0)
            scan_inside(0, range(1, 6))
            project_out("g_kv", kv3)
            scan_inside(0, range(6, 14))
            project_out("g_u1", u3[:, 4:8, :])
            dve.wait_ge(rsqrt_ready, 1)
            nc.vector.scalar_tensor_tensor(kv3[:, 0:2, :], kv3[:, 0:2, :], small[:, SMALL["g_k"]],
                                           sq3[:, 0:2, :], ALU.mult, ALU.mult).then_inc(k_ready, 1)
            link(nc.vector.tensor_scalar(stat[:, 48:49], small[:, SMALL["g_q"]], HEAD_DIM ** -0.5, None, ALU.mult))
            scan_inside(0, range(14, 16))
            scan_across(0, range(1, 8))
            project_out("g_q0", q3[:, 0:4, :])
            scan_across(0, range(8, ACROSS_BEFORE_Q1))
            project_out("g_q1", q3[:, 4:8, :])
            scan_across(0, range(ACROSS_BEFORE_Q1, CHUNK))
            for m, buf in ((0, sq3), (1, au3)):
                dve.wait_ge(rsqrt_ready, 2 + m)
                nc.vector.scalar_tensor_tensor(q3[:, 4 * m:4 * m + 4, :], q3[:, 4 * m:4 * m + 4, :],
                                               stat[:, 48:49], buf, ALU.mult, ALU.mult).then_inc(q_ready, 1)
            dve.wait_ge(q_blk_zero, 1)
            dve.wait_ge(q_ready, 2)
            for half in range(2):
                rows = slice(64 * half, 64 * half + 64)
                for g in range(2):
                    src = q3[rows, 4 * g:4 * g + 4, SEQ:TOK].rearrange("p r (n i) -> p n r i", i=DEC_SEQ)
                    dst = qb4[rows, g, :, 16 * half:16 * half + 16].rearrange("p n (r i) -> p n r i", i=DEC_SEQ)
                    copied = nc.vector.tensor_copy(dst, src)
            copied.then_inc(qblk_ready, 1)

            def y_out(half):
                u = UNIT[f"y{half}"]
                unit_full(dve, u)
                for o in range(4):
                    q = 4 * half + o
                    at = SMALL["d_skip"].start + q
                    done = nc.vector.scalar_tensor_tensor(u3[:, q, :], u3[:, q, :], small[:, at:at + 1],
                                                          banks(u)[:, o, :], ALU.mult, ALU.add)
                done.then_inc(evacuated[u % 2], 1)

            delta = const[:, CONST["delta"]]

            def soft_max(i):
                u = UNIT[f"sc{i}"]
                unit_full(dve, u)
                for b in range(4):
                    t, half = 2 * i + b // 2, b % 2
                    head = (2 * (t // 4) + half) * Q_PER_KV + t % 4
                    biased = nc.vector.scalar_tensor_tensor(sh3[:, b, :], delta, SLOPES[head],
                                                            banks(u, 4, 384)[:, b, :], ALU.mult, ALU.add)
                biased.then_inc(evacuated[u % 2], 1)
                unit_read(dve, u)
                link(nc.vector.tensor_reduce(stat[:, 0:4], sh3[:, :, 0:128], AX.X, ALU.max))
                link(nc.vector.tensor_reduce(stat[:, 4:8], sh3[:, :, 128:384], AX.X, ALU.max))
                linked()
                m = stat[:, 0:8].rearrange("p (k b) -> p k b", k=2)
                at = SMALL["sinks"].start + 4 * i
                sink = small[:, at:at + 4].unsqueeze(1).to_broadcast([P, 2, 4])
                link(tt(m, m, sink, ALU.max))
                linked()
                link(nc.vector.tensor_scalar(stat[:, 8:16], stat[:, 0:8], -1.0, None, ALU.mult))
                linked()
                tt(stat[:, 24:32].rearrange("p (k b) -> p k b", k=2), sink,
                   stat[:, 8:16].rearrange("p (k b) -> p k b", k=2), ALU.add).then_inc(max_ready, 1)

            def invert_sum(n_softmax):
                dve.wait_ge(exp_ready, n_softmax)
                link(tt(stat[:, 16:24], stat[:, 16:24], stat[:, 24:32], ALU.add))
                linked()
                nc.vector.reciprocal(stat[:, 16:24], stat[:, 16:24]).then_inc(sum_inverted, 1)

            def sample_max():
                u = UNIT["ssc"]
                unit_full(dve, u)
                dve.wait_ge(bias_loaded, 16)
                bias = sample_bias[:, :].rearrange("p (b s) -> p b s", b=4)
                tt(ss3, banks(u, 4, SAMPLE_KEYS), bias, ALU.add).then_inc(evacuated[u % 2], 1)
                unit_read(dve, u)
                link(nc.vector.tensor_reduce(stat[:, 32:36], ss3, AX.X, ALU.max))
                linked()
                sink = small[:, SMALL["sink_rows"]].unsqueeze(2).to_broadcast([P, 2, 2])
                m = stat[:, 32:36].rearrange("p (g b) -> p g b", g=2)
                link(tt(m, m, sink, ALU.max))
                linked()
                link(nc.vector.tensor_scalar(stat[:, 36:40], stat[:, 32:36], -1.0, None, ALU.mult))
                linked()
                tt(stat[:, 44:48].rearrange("p (g b) -> p g b", g=2), sink,
                   stat[:, 36:40].rearrange("p (g b) -> p g b", g=2), ALU.add).then_inc(max_ready, 1)

            def invert_sample_sum():
                dve.wait_ge(exp_ready, 2)
                link(tt(stat[:, 40:44], stat[:, 40:44], stat[:, 44:48], ALU.add))
                linked()
                nc.vector.reciprocal(stat[:, 40:44], stat[:, 40:44]).then_inc(sum_inverted, 1)

            def mix_sum(m):
                dve.wait_ge(mix_squared, m + 1)
                if m % 2 == 0:
                    nc.vector.tensor_reduce(ssq[:, :], sq3.rearrange("p k t -> p t k"), AX.X, ALU.add) \
                        .then_inc(mix_summed, 1)
                else:
                    link(nc.vector.tensor_reduce(ssq_part[:, :], sq3.rearrange("p k t -> p t k"), AX.X, ALU.add))
                    linked()
                    tt(ssq[:, :], ssq[:, :], ssq_part[:, :], ALU.add).then_inc(mix_summed, 1)
                    dve.wait_ge(mix_summed, m + 1)

            def mix_lo_part(m, dst, hi):
                dve.wait_ge(mix_hi, m + 1)
                dve.wait_ge(mix_gained, m + 1)
                tt(dst, au3, hi.bitcast(F32), ALU.subtract).then_inc(mix_lo, 1)

            def attention_out(g):
                u = UNIT[f"pv{g}"]
                if g:
                    dve.wait_ge(mix_lo, g)
                dve.wait_ge(evacuated[u % 2], evacuations(u) - 1)
                tt(au3[:, :, 0:SEQ], banks(u, 4, SEQ), gain("g_attn", slice(4 * g, 4 * g + 4), SEQ), ALU.mult) \
                    .then_inc(evacuated[u % 2], 1)
                unit_read(dve, UNIT["spv"])
                tt(au3[:, :, SEQ:TOK].rearrange("p r (n i) -> p r n i", i=DEC_SEQ),
                   so3[:, g, :].rearrange("p (n r i) -> p r n i", r=Q_PER_KV, i=DEC_SEQ),
                   gain("g_attn", slice(4 * g, 4 * g + 4), DEC_BATCH).unsqueeze(3)
                   .to_broadcast([P, Q_PER_KV, DEC_BATCH, DEC_SEQ]), ALU.mult).then_inc(mix_gained, 1)
                mix_sum(g)
                mix_lo_part(g, a4[:, 4 * g:4 * g + 4, 1, :], a4[:, 4 * g:4 * g + 4, 0, :])

            done = [0]

            def scan_more(n):
                for k in range(done[0], min(done[0] + n, 2 * (CHUNK - 1))):
                    if k < CHUNK - 1:
                        scan_inside(1, [k + 1])
                    else:
                        scan_across(1, [k - CHUNK + 2])
                done[0] += n

            soft_max(0)
            sample_max()
            y_out(0)
            invert_sum(1)
            invert_sample_sum()
            dve.wait_ge(last_copied, 1)
            bu_out(1)
            states_there(1)
            scan_sample(1)
            soft_max(1)
            scan_more(1)
            invert_sum(3)
            scan_more(4)
            soft_max(2)
            scan_more(1)
            invert_sum(4)
            scan_more(1)
            attention_out(0)
            scan_more(2)
            soft_max(3)
            scan_more(1)
            invert_sum(5)
            scan_more(4)
            attention_out(1)
            scan_more(2)

            def scale_out(name, m):
                u = UNIT[name]
                unit_full(dve, u)
                if m >= 2:
                    dve.wait_ge(added, m - 1)
                tt(tb4[:, m % 2, :, :], banks(u), over_tiles(r_b[:, :], OUTS), ALU.mult) \
                    .then_inc(evacuated[u % 2], 1)

            one_over_root(UNIT["rms_a"])
            scale_out("wa0", 0)
            scan_more(4)
            scale_out("wa1", 1)
            scan_more(4)
            scale_out("wa2", 2)
            scan_more(4)
            scale_out("wa3", 3)
            scan_more(30)
            lo_parts(range(56, 60))
            y_out(1)
            for m in range(2):
                dve.wait_ge(g_hi, m + 1)
                tt(a4[:, 8 + 4 * m:12 + 4 * m, 1, :], u3[:, 4 * m:4 * m + 4, :],
                   a4[:, 8 + 4 * m:12 + 4 * m, 0, :].bitcast(F32), ALU.subtract).then_inc(g_lo, 1)
            for m in range(2):
                lo_parts(range(60 + 4 * m, 64 + 4 * m))
                unit_read(dve, UNIT[f"glu{m}"])
                dve.wait_ge(mix_lo, 2 + m)
                tt(au3, u3[:, 4 * m:4 * m + 4, :], tb4[:, m, :, :], ALU.mult).then_inc(mix_raw, 1)
                dve.wait_ge(mix_squared, 2 + m + 1)
                tt(au3, au3, gain("g_ssm", slice(4 * m, 4 * m + 4)), ALU.mult).then_inc(mix_gained, 1)
                mix_sum(2 + m)
                mix_lo_part(2 + m, b4[:, 4 * m:4 * m + 4, 1, :], b4[:, 4 * m:4 * m + 4, 0, :])
            lo_parts(range(68, 72))
            one_over_root(UNIT["rms_s"])

            def residual_out(g):
                scale_out(f"ws{g}", 4 + g)
                dve.wait_ge(added, 4 + g + 1)
                if g == 0:
                    dve.wait_ge(mix_lo, 4)
                else:
                    dve.wait_ge(h_lo, g)
                tt(au3, h3[:, 4 * g:4 * g + 4, :], gain("g_mlp", slice(4 * g, 4 * g + 4)), ALU.mult) \
                    .then_inc(h_gained, 1)
                dve.wait_ge(h_squared, g + 1)
                if g == 0:
                    unit_full(dve, UNIT["rms_s"])
                    nc.vector.tensor_reduce(ssq[:, :], sq3.rearrange("p k t -> p t k"), AX.X, ALU.add) \
                        .then_inc(h_summed, 1)
                else:
                    link(nc.vector.tensor_reduce(ssq_part[:, :], sq3.rearrange("p k t -> p t k"), AX.X, ALU.add))
                    linked()
                    tt(ssq[:, :], ssq[:, :], ssq_part[:, :], ALU.add).then_inc(h_summed, 1)
                dve.wait_ge(h_hi, g + 1)
                tt(a4[:, 4 * g:4 * g + 4, 1, :], au3, a4[:, 4 * g:4 * g + 4, 0, :].bitcast(F32), ALU.subtract) \
                    .then_inc(h_lo, 1)

            for g in range(4):
                if g:
                    lo_parts(range(68 + 4 * g, 72 + 4 * g))
                residual_out(g)

            def mlp_lo(group, past=0, last=False):
                n = S_MLP + GROUP_STEPS * group + SLOTS
                lo_parts(range(n, n + GROUP_STEPS - (SLOTS if last else 0)), past)

            def up_out(unit, g, past=0, split_before=0):
                unit_full(dve, unit, past)
                if g >= 2:
                    dve.wait_ge(hid_lo, past * 4 + (split_before + g - 1))
                nc.vector.tensor_scalar(sr4[:, g % 2, :, :], banks(unit), 0.0, None, ALU.max) \
                    .then_inc(evacuated[unit % 2], 1)
                unit_read(dve, unit, past)
                tt(sr4[:, g % 2, :, :], sr4[:, g % 2, :, :], sr4[:, g % 2, :, :], ALU.mult) \
                    .then_inc(hid_ready, 1)

            def down_out(g, past=0):
                unit = N_UNITS + g
                unit_full(dve, unit, past)
                dve.wait_ge(added, past * 4 + (8 + g - 1))
                tt(tb4[:, g % 2, :, :], banks(unit), over_tiles(r_b[:, :], OUTS), ALU.mult) \
                    .then_inc(evacuated[unit % 2], 1)

            for g in range(4):
                mlp_lo(g)
                up_out(UNIT[f"up{g}"], g)
                if g == 1:
                    one_over_root(UNIT["rms_h"])
                    link(tt(r_b[:, :], r_b[:, :], r_b[:, :], ALU.mult))
                    linked()
            with dve.Fori(0, N_BLOCKS - 1) as b:
                for g in range(4):
                    mlp_lo(4 + g, b)
                    down_out(g, b)
                for g in range(4):
                    mlp_lo(8 + g, b)
                    up_out(N_UNITS + 4 + g, g, b, split_before=4)
            for g in range(4):
                mlp_lo(4 + g, N_BLOCKS - 1, last=g == 3)
                down_out(g, N_BLOCKS - 1)

        @block.gpsimd
        def _(pool):
            own = [0]

            def link(ins_):
                own[0] += 1
                ins_.then_inc(pool_done, 1)

            def linked():
                pool.wait_ge(pool_done, own[0])

            def tt(out, x, y, op):
                return nc.gpsimd.tensor_tensor(out, x, y, op)

            pool.wait_ge(disc_ready, 1)
            pool.wait_ge(b_loaded, 16)

            def coef(k):
                return disc3[:, k, :].unsqueeze(1).unsqueeze(3).to_broadcast([P, 2, PAIRS, 32])

            link(tt(bbar4, bnat4, coef(CR), ALU.mult))
            linked()
            link(tt(bnat4, bnat4, coef(CI), ALU.mult))
            linked()
            link(tt(bbar4[:, 0, :, :], bbar4[:, 0, :, :], bnat4[:, 1, :, :], ALU.subtract))
            tt(bbar4[:, 1, :, :], bbar4[:, 1, :, :], bnat4[:, 0, :, :], ALU.add).then_inc(bbar_ready, 1)

            link(nc.gpsimd.tensor_copy(pw4[:, 0, :, 0], disc3[:, ABR, :]))
            link(nc.gpsimd.tensor_copy(pw4[:, 1, :, 0], disc3[:, ABI, :]))
            link(nc.gpsimd.tensor_scalar(pw4[:, 2, :, 0], disc3[:, ABI, :], -1.0, None, ALU.mult))
            linked()
            pool.wait_ge(x_lo, 4)
            n = 1
            while n < CHUNK:
                base = [pw4[:, k, :, n - 1].unsqueeze(1).unsqueeze(3).to_broadcast([P, 2, PAIRS, n])
                        for k in range(2)]
                prod = [x_g[:, k * 512:k * 512 + 64 * n].rearrange("p (r j s) -> p r j s", r=2, s=n)
                        for k in range(2)]
                old = pw4[:, 0:2, :, 0:n]
                link(tt(prod[0], old, base[0], ALU.mult))
                link(tt(prod[1], old, base[1], ALU.mult))
                linked()
                link(tt(pw4[:, 0, :, n:2 * n], prod[0][:, 0, :, :], prod[1][:, 1, :, :], ALU.subtract))
                link(tt(pw4[:, 1, :, n:2 * n], prod[0][:, 1, :, :], prod[1][:, 0, :, :], ALU.add))
                linked()
                minus_im = nc.gpsimd.tensor_scalar(pw4[:, 2, :, n:2 * n], pw4[:, 1, :, n:2 * n], -1.0, None,
                                                   ALU.mult)
                if 2 * n == CHUNK:
                    minus_im.then_inc(powers_ready, 1)
                else:
                    link(minus_im)
                    linked()
                n *= 2

            def lo_parts(steps):
                for n in steps:
                    pool.wait_ge(hi_split, n + 1)
                    tt(lo3[:, n % SLOTS, :], raw3[:, n % SLOTS, :], hi3[:, n % SLOTS, :].bitcast(F32),
                       ALU.subtract).then_inc(lo_split[n % SLOTS], 1)

            def copy_last(half):
                pool.wait_ge(scanned, half + 1)
                if half:
                    unit_full(pool, UNIT["spv"])
                for r in range(2):
                    copied = nc.gpsimd.tensor_copy(last4[half][:, r, :, :], st4[:, r, :, SEQ - 1:TOK:DEC_SEQ])
                copied.then_inc(last_copied, 1)

            def add_group(g, unit, buf, past=0):
                unit_read(pool, unit, past)
                tt(h3[:, 4 * g:4 * g + 4, :], h3[:, 4 * g:4 * g + 4, :], tb4[:, buf, :, :], ALU.add) \
                    .then_inc(added, 1)

            lo_parts(range(POOL_SPLITS.start, S_WA))
            unit_full(pool, UNIT["g_q1"])
            nc.gpsimd.memset(q_blk[:, :], 0.0).then_inc(q_blk_zero, 1)
            lo_parts(range(S_WA, S_WA + SLOTS))
            copy_last(0)
            for g in range(4):
                n = S_WA + SLOTS + 4 * g
                if g < 3:
                    lo_parts(range(n, n + 4))
                add_group(g, UNIT[f"wa{g}"], g % 2)
            copy_last(1)
            for g in range(4):
                add_group(g, UNIT[f"ws{g}"], g % 2)

            def relu_lo(g, past=0, split_before=0):
                pool.wait_ge(hid_hi, past * 4 + (split_before + g + 1))
                tt(b4[:, 4 * g:4 * g + 4, 1, :], sr4[:, g % 2, :, :], b4[:, 4 * g:4 * g + 4, 0, :].bitcast(F32),
                   ALU.subtract).then_inc(hid_lo, 1)

            for g in range(4):
                relu_lo(g)
            with pool.Fori(0, N_BLOCKS - 1) as b:
                for g in range(4):
                    add_group(g, N_UNITS + g, g % 2, b)
                for g in range(4):
                    relu_lo(g, b, split_before=4)
            for g in range(4):
                add_group(g, N_UNITS + g, g % 2, N_BLOCKS - 1)

        @block.tensor
        def _(pe):
            def mm(out, lhs_t, rhs, start=True, stop=True):
                return nc.tensor.matmul(out, lhs_t, rhs, start=start, stop=stop)

            def gemm(unit, first_step, n_steps, mov, tile0, past=0, past_units=0, ready=None, part=None):
                part = part or range(n_steps)
                if part.start == 0:
                    unit_free(pe, unit, past_units)
                for i in part:
                    n = first_step + i
                    pe.wait_ge(lo_split[n % SLOTS], past * (BLOCK_STEPS // SLOTS) + (n // SLOTS + 1))
                    for kk in range(STEP_K):
                        k = STEP_K * i + kk
                        if ready:
                            ready(k)
                        for o in range(OUTS):
                            out = banks(unit)[:, o, :]
                            w_h = hi4[:, n % SLOTS, kk, o * P:(o + 1) * P]
                            w_l = lo4[:, n % SLOTS, kk, o * P:(o + 1) * P]
                            x_h, x_l = mov[:, tile0 + k, 0, :], mov[:, tile0 + k, 1, :]
                            mm(out, w_h, x_h, start=k == 0, stop=False)
                            mm(out, w_h, x_l, start=False, stop=False)
                            last_mm = mm(out, w_l, x_h, start=False, stop=k == n_steps * STEP_K - 1)
                    last_mm.then_inc(step_used, 1)

            def parts_ready(signal, before=0):
                def ready(k):
                    if k % 4 == 0:
                        pe.wait_ge(signal, before + k // 4 + 1)
                return ready

            def sum_over_features(unit, signal, count):
                unit_free(pe, unit)
                pe.wait_ge(signal, count)
                mm(banks(unit, 1)[:, 0, :], ones, ssq[:, :]).then_inc(psum_full, 1)

            def project_pairs(half):
                unit_read(pe, UNIT["b_turn"])
                unit_read(pe, UNIT[f"g_u{half}"])
                for k in range(8):
                    u = UNIT[f"bu{half}_{k}"]
                    unit_free(pe, u)
                    for jj in range(2):
                        j = 16 * half + 2 * k + jj
                        rows = slice(32 * (j % 4), 32 * (j % 4) + 32)
                        for r in range(2):
                            done = mm(banks(u)[:, 2 * jj + r, :], bw4[rows, r, j // 4, :], u3[rows, j // 4, :])
                    done.then_inc(psum_full, 1)

            def project_states(half):
                u = UNIT[f"y{half}"]
                unit_free(pe, u)
                pe.wait_ge(scanned, half + 1)
                pe.wait_ge(c_ready, 1)
                for o in range(4):
                    for jj in range(4):
                        j = 16 * half + 4 * o + jj
                        out = psum[32 * jj:32 * jj + 32, 4 * (u % 2) + o, 0:TOK]
                        for r in range(2):
                            done = mm(out, c4[:, r, j, :], st4[:, r, j % 16, :], start=r == 0, stop=r == 1)
                done.then_inc(psum_full, 1)

            def head_means(name, squares, n):
                u = UNIT[name]
                unit_free(pe, u)
                for k in range(n):
                    done = mm(banks(u)[:, k, :], head_mean, squares[:, k, :])
                return done

            def scores(i):
                u = UNIT[f"sc{i}"]
                unit_free(pe, u)
                for b in range(4):
                    t, rows = 2 * i + b // 2, slice(64 * (b % 2), 64 * (b % 2) + 64)
                    out = banks(u, 4, 384)[:, b, :]
                    mm(out[:, 0:128], q3[rows, t, 0:128], kv3[rows, t // 4, 0:128])
                    done = mm(out[:, 128:384], q3[rows, t, 128:256], kv3[rows, t // 4, 0:256])
                done.then_inc(psum_full, 1)

            def turn_probs(i, n_softmax):
                u = UNIT[f"pt{i}"]
                unit_free(pe, u)
                pe.wait_ge(probs_ready, n_softmax)
                for b in range(4):
                    for k in range(3):
                        cols = slice(128 * k, 128 * k + 128)
                        done = nc.tensor.transpose(banks(u, 4, 384)[:, b, cols], sh3[:, b, cols], ident)
                done.then_inc(psum_full, 1)

            def attend(g):
                u = UNIT[f"pv{g}"]
                unit_free(pe, u)
                unit_read(pe, UNIT[f"pt{2 * g}"])
                unit_read(pe, UNIT[f"pt{2 * g + 1}"])
                for r in range(4):
                    for half in range(2):
                        rows = slice(64 * half, 64 * half + 64)
                        cols = slice(64 * (2 * g + half), 64 * (2 * g + half) + 64)
                        probs = pt4[:, r // 2, 2 * (r % 2) + half, :]
                        out = psum[rows, 4 * (u % 2) + r, 0:SEQ]
                        mm(out[:, 0:128], v3[:, 0, cols], probs[:, 0:128])
                        mm(out[:, 128:256], v3[:, 0, cols], probs[:, 128:256], stop=False)
                        done = mm(out[:, 128:256], v3[:, 1, cols], probs[:, 256:384], start=False)
                done.then_inc(psum_full, 1)

            gemm(UNIT["g_u0"], S_U0, GROUP_STEPS, a4, 0, ready=parts_ready(x_lo), part=range(6))
            pe.wait_ge(const_loaded, 16)
            sum_over_features(UNIT["rms_x"], x_summed, 1)
            u = UNIT["b_turn"]
            unit_free(pe, u)
            pe.wait_ge(bbar_ready, 1)
            for r in range(2):
                for q in range(QT):
                    turned = nc.tensor.transpose(
                        banks(u, 4, 512)[:, 2 * r + q // 4, (q % 4) * P:(q % 4 + 1) * P],
                        bbar4[:, r, 4 * q:4 * q + 4, :].rearrange("p j c -> p (j c)"), ident)
            turned.then_inc(psum_full, 1)
            gemm(UNIT["g_u0"], S_U0, GROUP_STEPS, a4, 0, part=range(6, GROUP_STEPS))
            project_pairs(0)
            gemm(UNIT["g_kv"], S_KV, GROUP_STEPS, a4, 0)
            gemm(UNIT["g_u1"], S_U1, GROUP_STEPS, a4, 0)
            pe.wait_ge(squared, 1)
            head_means("kv_aux", sq3, 2)
            b0 = 4 * (UNIT["kv_aux"] % 2)
            for g in range(2):
                for t in range(2):
                    nc.tensor.transpose(psum[:, b0 + 2, t * KV_WIDTH + g * P:t * KV_WIDTH + (g + 1) * P],
                                        kv3[:, 2 + g, t * P:(t + 1) * P], ident)
                turned = nc.tensor.transpose(psum[0:SAMPLE, b0 + 3, g * P:(g + 1) * P],
                                             kv3[:, 2 + g, SEQ:TOK], ident)
            turned.then_inc(psum_full, 1)
            gemm(UNIT["g_q0"], S_Q0, GROUP_STEPS, a4, 0)
            gemm(UNIT["g_q1"], S_Q1, GROUP_STEPS, a4, 0, part=range(4))
            pe.wait_ge(squared, 2)
            head_means("qn0", sq3, 4).then_inc(psum_full, 1)
            gemm(UNIT["g_q1"], S_Q1, GROUP_STEPS, a4, 0, part=range(4, GROUP_STEPS))
            pe.wait_ge(squared, 3)
            head_means("qn1", au3, 4).then_inc(psum_full, 1)
            pe.wait_ge(k_ready, 1)
            pe.wait_ge(q_ready, 1)
            scores(0)
            u = UNIT["ssc"]
            unit_free(pe, u)
            pe.wait_ge(qblk_ready, 1)
            pe.wait_ge(kc_loaded, 16)
            for g in range(2):
                for n in range(DEC_BATCH):
                    out = psum[32 * (n % 4):32 * (n % 4) + 32, 4 * (u % 2) + 2 * g + n // 4, :]
                    mm(out[:, 0:WINDOW], qb4[:, g, n, :], kc4[:, g, n, :])
                    done = mm(out[:, WINDOW:WINDOW + SAMPLE], qb4[:, g, n, :], kv3[:, g, SEQ:TOK])
            done.then_inc(psum_full, 1)
            project_states(0)
            project_pairs(1)
            turn_probs(0, 1)
            scores(1)
            u = UNIT["spt"]
            unit_free(pe, u)
            pe.wait_ge(probs_ready, 2)
            for b in range(4):
                nc.tensor.transpose(psum[:, 4 * (u % 2), b * P:(b + 1) * P], ss3[:, b, 0:WINDOW], ident)
                turned = nc.tensor.transpose(psum[0:SAMPLE, 4 * (u % 2) + 1, b * P:(b + 1) * P],
                                             ss3[:, b, WINDOW:WINDOW + SAMPLE], ident)
            turned.then_inc(psum_full, 1)
            turn_probs(1, 3)
            pe.wait_ge(q_ready, 2)
            scores(2)
            attend(0)
            u = UNIT["spv"]
            unit_free(pe, u)
            unit_read(pe, UNIT["spt"])
            pe.wait_ge(vc_loaded, 16)
            for g in range(2):
                for half in range(2):
                    cols = slice(64 * (2 * g + half), 64 * (2 * g + half) + 64)
                    out = psum[64 * half:64 * half + 64, 4 * (u % 2) + g, 0:P]
                    mm(out, v3[0:SAMPLE, 2, cols], ptn[0:SAMPLE, g, :, half, :], stop=False)
                    for n in range(DEC_BATCH):
                        done = mm(out[:, 16 * n:16 * n + 16], vc3[:, n, cols], pts[:, g, n, half, :],
                                  start=False, stop=n == DEC_BATCH - 1)
            done.then_inc(psum_full, 1)
            turn_probs(2, 4)
            scores(3)
            turn_probs(3, 5)
            attend(1)
            gemm(UNIT["wa0"], S_WA, HALF_STEPS, a4, 0, ready=parts_ready(mix_lo))
            sum_over_features(UNIT["rms_a"], mix_summed, 2)
            for g in range(1, 4):
                gemm(UNIT[f"wa{g}"], S_WA + HALF_STEPS * g, HALF_STEPS, a4, 0)
            project_states(1)
            gemm(UNIT["glu0"], S_GLU, HALF_STEPS, a4, QT, ready=parts_ready(g_lo))
            gemm(UNIT["glu1"], S_GLU + HALF_STEPS, HALF_STEPS, a4, QT)
            gemm(UNIT["ws0"], S_WS, HALF_STEPS, b4, 0, ready=parts_ready(mix_lo, 2))
            sum_over_features(UNIT["rms_s"], mix_summed, 4)
            for g in range(1, 4):
                gemm(UNIT[f"ws{g}"], S_WS + HALF_STEPS * g, HALF_STEPS, b4, 0)
            for g in range(2):
                gemm(UNIT[f"up{g}"], S_MLP + GROUP_STEPS * g, GROUP_STEPS, a4, 0,
                     ready=parts_ready(h_lo) if g == 0 else None)
            sum_over_features(UNIT["rms_h"], h_summed, 4)
            for g in range(2, 4):
                gemm(UNIT[f"up{g}"], S_MLP + GROUP_STEPS * g, GROUP_STEPS, a4, 0)

            def block_groups(kind, b):
                first, unit, mov = (4, N_UNITS, b4) if kind == "down" else (8, N_UNITS + 4, a4)

                for g in range(4):
                    def ready(k, g=g):
                        if kind == "down" and g == 0 and k % 4 == 0:
                            pe.wait_ge(hid_lo, b * 4 + (k // 4 + 1))
                    gemm(unit + g, S_MLP + GROUP_STEPS * (first + g), GROUP_STEPS, mov, 0, b, b, ready)

            with pe.Fori(0, N_BLOCKS - 1) as b:
                block_groups("down", b)
                block_groups("up", b)
            block_groups("down", N_BLOCKS - 1)


_OUTS = {
    "y": (P, KT * TOK),
    "kv": (P, OUTS * TOK),
    "kc": (P, 2, DEC_BATCH, WINDOW - DEC_SEQ),
    "vc": (DEC_BATCH, WINDOW - DEC_SEQ, KV_WIDTH),
    "last": (2, P, 2 * 16 * 9),
}


def _tiles(a, tiles):
    return a.reshape((tiles, P) + a.shape[1:]).swapaxes(0, 1)


def _lay_out(x):
    f = np.float32
    heads = [(2 * g + half) * Q_PER_KV + r for g in range(2) for r in range(Q_PER_KV) for half in range(2)]
    head_order = np.concatenate([np.arange(h * HEAD_DIM, (h + 1) * HEAD_DIM) for h in heads])
    o_k, o_u = ATTN_WIDTH, ATTN_WIDTH + 2 * KV_WIDTH

    def steps(w):
        return w.reshape(-1, STEP_K, P, STEP_N).transpose(0, 2, 1, 3).reshape(-1, P, STEP_COLS)

    w_in, w_out, w_glu = x["w_in"][0], x["w_out"][0], x["w_glu"][0]
    up, down = x["w_mlp_up"][0], x["w_mlp_down"][0]
    w = np.empty((N_STEPS, P, STEP_COLS), f)
    q_cols = w_in[:, :ATTN_WIDTH][:, head_order]
    w[S_U0:S_KV] = steps(w_in[:, o_u:o_u + 512])
    w[S_KV:S_U1] = steps(w_in[:, o_k:o_u])
    w[S_U1:S_Q0] = steps(w_in[:, o_u + 512:])
    w[S_Q0:S_Q1] = steps(q_cols[:, :512])
    w[S_Q1:S_WA] = steps(q_cols[:, 512:])
    wa, ws = w_out[:ATTN_WIDTH][head_order], w_out[ATTN_WIDTH:]
    for g in range(4):
        cols = slice(g * STEP_N, (g + 1) * STEP_N)
        w[S_WA + 4 * g:S_WA + 4 * g + 4] = steps(wa[:, cols])
        w[S_WS + 4 * g:S_WS + 4 * g + 4] = steps(ws[:, cols])
        if g < 2:
            w[S_GLU + 4 * g:S_GLU + 4 * g + 4] = steps(w_glu[:, cols])
    for b in range(N_BLOCKS):
        for g in range(4):
            at = S_MLP + b * BLOCK_STEPS + g * GROUP_STEPS
            w[at:at + GROUP_STEPS] = steps(up[:, b * D_MODEL + g * STEP_N:b * D_MODEL + (g + 1) * STEP_N])
            at += 4 * GROUP_STEPS
            w[at:at + GROUP_STEPS] = steps(down[b * D_MODEL:(b + 1) * D_MODEL, g * STEP_N:(g + 1) * STEP_N])

    tokens = np.concatenate([x["x_prompt"][0], x["x_sample"].reshape(SAMPLE, D_MODEL)])
    small = np.zeros((P, N_SMALL), f)

    def put(name, value):
        small[:, SMALL[name]] = value

    put("g_in", _tiles(x["attn_norm_g"][0], KT))
    put("g_mlp", _tiles(x["mlp_norm_g"][0], KT))
    put("g_attn", _tiles(x["attn_out_g"][0][head_order], QT))
    put("g_ssm", _tiles(x["ssm_out_g"][0], QT))
    put("d_skip", _tiles(x["ssm_D"][0], QT))
    put("b_glu", _tiles(x["b_glu"][0], QT))
    put("g_q", np.concatenate([x["q_norm_g"][0]] * 2)[:, None])
    put("g_k", np.concatenate([x["k_norm_g"][0]] * 2)[:, None])
    sinks = x["attn_sinks"][0]
    put("sinks", np.broadcast_to(sinks[heads], (P, N_HEADS)))
    by_row = sinks.reshape(2, 2, Q_PER_KV)
    put("sink_rows", np.broadcast_to(by_row[None, :, :, :, None], (4, 2, 2, Q_PER_KV, DEC_SEQ))
        .transpose(0, 2, 3, 4, 1).reshape(P, 2))
    put("a_re", x["ssm_A_re"][0].reshape(PAIRS, P).T)
    put("a_im", x["ssm_A_im"][0].reshape(PAIRS, P).T)
    put("log_dt", np.repeat(x["ssm_log_dt"][0].reshape(PAIRS, 2), STATE_DIM, axis=1).T)
    put("eps", EPS)
    h0 = np.stack([x["state_ssm_re"][0], x["state_ssm_im"][0]])
    put("h0", h0.reshape(2, DEC_BATCH, PAIRS, P).transpose(3, 0, 2, 1).reshape(P, -1))

    def by_state(b):
        out = np.zeros((2, STATE_DIM, PAIRS, 2, SSM_GROUP), f)
        b = b.reshape(PAIRS, 2, STATE_DIM, SSM_GROUP)
        for k in range(2):
            out[k, :, :, k, :] = b[:, k].transpose(1, 0, 2)
        return out.reshape(P, PAIRS * 32)

    b_in = np.concatenate([by_state(x["ssm_B_re"][0]), by_state(x["ssm_B_im"][0])], axis=1)
    c_in = np.concatenate([by_state(x[n][0].transpose(0, 2, 1)) for n in ("ssm_C_re", "ssm_C_im")], axis=1)
    kc = x["cache_k"][0].reshape(DEC_BATCH, WINDOW, 2, P).transpose(3, 2, 0, 1).reshape(P, -1)
    vc = x["cache_v"][0].reshape(DEC_BATCH, WINDOW, KV_WIDTH)
    laid = {"w": w, "x": tokens.T.reshape(KT, P, TOK).transpose(1, 0, 2).reshape(P, -1), "small": small,
            "b": b_in, "c": c_in, "kc": kc, "vc": vc, "const": _constants(),
            "sample_bias": _sample_bias()}
    return {k: np.ascontiguousarray(v) for k, v in laid.items()}


def _constants():
    const = np.zeros((P, N_CONST), np.float32)
    const[:, CONST["ident"]] = np.eye(P)
    const[:, CONST["ones"]] = 1.0
    const[:, CONST["head_mean"]] = np.kron(np.eye(2), np.ones((HEAD_DIM, HEAD_DIM))) / HEAD_DIM
    i, j = np.arange(P)[:, None], np.arange(P)[None, :]
    own = np.where(j <= i, -(i - j), MASKED)
    before = np.where(j >= i, -(i + P - j), MASKED)
    const[:, CONST["delta"]] = np.concatenate([own, before, own], axis=1)
    return const


def _sample_bias():
    bias = np.full((4, 2, Q_PER_KV, DEC_SEQ, 2, 2, SAMPLE_KEYS), MASKED)
    for n4, half, r, i, g, nb in np.ndindex(4, 2, Q_PER_KV, DEC_SEQ, 2, 2):
        slope = SLOPES[(2 * g + half) * Q_PER_KV + r]
        row = bias[n4, half, r, i, g, nb]
        for j in range(i, WINDOW):
            row[j] = -slope * (i + WINDOW - j)
        for j in range(i + 1):
            row[WINDOW + (4 * nb + n4) * DEC_SEQ + j] = -slope * (i - j)
    return bias.reshape(P, 4 * SAMPLE_KEYS).astype(np.float32)


def kernel(**inputs):
    import concourse.bacc as bacc
    from concourse.bass_utils import run_bass_kernel_spmd

    arrays = _lay_out({k: np.asarray(v) for k, v in inputs.items()})
    nc = bacc.Bacc("TRN2", target_bir_lowering=False, num_devices=1)
    ins = {k: nc.dram_tensor(f"in_{k}", a.shape, F32, kind="ExternalInput").ap() for k, a in arrays.items()}
    outs = {k: nc.dram_tensor(f"out_{k}", shape, F32, kind="ExternalOutput").ap() for k, shape in _OUTS.items()}
    build_program(nc, ins, outs)
    res = run_bass_kernel_spmd(nc, [{f"in_{k}": a for k, a in arrays.items()}], core_ids=[0]).results[0]
    y, kv, kc, vc, last = (res[f"out_{k}"] for k in _OUTS)

    y = y.reshape(P, KT, TOK).transpose(2, 1, 0).reshape(TOK, D_MODEL)
    kv = kv.reshape(P, 2, 2, TOK).transpose(3, 1, 2, 0).reshape(TOK, 2, N_KV_HEADS, HEAD_DIM)
    new_prompt = [kv[SEQ - WINDOW:SEQ, c][None, None] for c in range(2)]
    kept_k = kc.transpose(2, 3, 1, 0).reshape(DEC_BATCH, WINDOW - DEC_SEQ, N_KV_HEADS, HEAD_DIM)
    kept_v = vc.reshape(DEC_BATCH, WINDOW - DEC_SEQ, N_KV_HEADS, HEAD_DIM)
    new_sample = [np.concatenate([kept, kv[SEQ:, c].reshape(DEC_BATCH, DEC_SEQ, N_KV_HEADS, HEAD_DIM)], axis=1)[None]
                  for c, kept in enumerate((kept_k, kept_v))]
    states = last.reshape(2, 2, STATE_DIM, 2, PAIRS // 2, 9).transpose(3, 5, 0, 4, 1, 2) \
        .reshape(2, 9, N_GROUPS, STATE_DIM)
    out = (y[:SEQ][None], y[SEQ:].reshape(DEC_BATCH, DEC_SEQ, D_MODEL), new_prompt[0], new_prompt[1],
           states[0, :1][None], states[1, :1][None], new_sample[0], new_sample[1],
           states[0, 1:][None], states[1, 1:][None])
    return tuple(np.ascontiguousarray(a) for a in out)
```
